# Optimizing a Trainium2 kernel written in Bass

```python
import jax, jax.numpy as jnp
from jax import lax
import numpy as np

D_MODEL = 2048
BATCH = 1
SEQ = 256
DEPTH = 1

N_META = 16
D_LRU = D_MODEL // 2
N_LRU_HEADS = 16
LRU_BLOCK = D_LRU // N_LRU_HEADS
LRU_CONV_WIDTH = 4
LRU_C = 8.0
D_SCONV = D_MODEL - D_LRU
N_SCONV_GROUPS = 16
SCONV_BLOCK = D_SCONV // N_SCONV_GROUPS
SCONV_WIDTH = 3
D_FF = ((8 * D_MODEL // 3 + 127) // 128) * 128
IN_COLS = 2 * D_LRU + 3 * D_SCONV
EPS = 1e-6

kernel_name = "hymba_lru_shortconv_macaron"

def rmsnorm(x, g):
    xf = x.astype(jnp.float32)
    y = xf * lax.rsqrt(jnp.mean(xf * xf, axis=-1, keepdims=True) + EPS)
    return (y * g.astype(jnp.float32)).astype(x.dtype)

def group_rmsnorm(x, g, n_groups):
    b, t, c = x.shape
    xf = x.astype(jnp.float32).reshape(b, t, n_groups, c // n_groups)
    y = xf * lax.rsqrt(jnp.mean(xf * xf, axis=-1, keepdims=True) + EPS)
    return (y.reshape(b, t, c) * g.astype(jnp.float32)).astype(x.dtype)

def causal_depthwise_conv(x, w):
    k = w.shape[0]
    return lax.conv_general_dilated(
        x, w[:, None, :].astype(x.dtype), window_strides=(1,),
        padding=[(k - 1, 0)], dimension_numbers=("NWC", "WIO", "NWC"),
        feature_group_count=x.shape[-1])

def swiglu(x, w_gate, w_up, w_down):
    return (jax.nn.silu(x @ w_gate) * (x @ w_up)) @ w_down

def rg_lru(x, w_a, b_a, w_x, b_x, lam):
    bn, t, c = x.shape
    xh = x.reshape(bn, t, N_LRU_HEADS, LRU_BLOCK)
    gate_a = jax.nn.sigmoid(jnp.einsum("bthi,hij->bthj", xh, w_a).reshape(bn, t, c) + b_a)
    gate_x = jax.nn.sigmoid(jnp.einsum("bthi,hij->bthj", xh, w_x).reshape(bn, t, c) + b_x)
    log_a = -LRU_C * gate_a.astype(jnp.float32) * jax.nn.softplus(-lam.astype(jnp.float32))
    a = jnp.exp(log_a)
    mult = jnp.sqrt(-jnp.expm1(2.0 * log_a))
    u = mult * (gate_x * x).astype(jnp.float32)

    def combine(left, right):
        a_l, b_l = left
        a_r, b_r = right
        return a_r * a_l, a_r * b_l + b_r

    _, h = lax.associative_scan(combine, (a, u), axis=1)
    return h.astype(x.dtype)

def setup_inputs(seed: int = 0) -> dict:
    key = jax.random.key(seed)
    ks = iter(jax.random.split(key, 40))
    f32 = jnp.float32
    L = DEPTH

    def nrm(shape, fan_in):
        return jax.random.normal(next(ks), shape, f32) * (fan_in ** -0.5)

    def gain(shape):
        return 1.0 + 0.02 * jax.random.normal(next(ks), shape, f32)

    def bias(shape):
        return 0.01 * jax.random.normal(next(ks), shape, f32)

    x = jax.random.normal(next(ks), (BATCH, SEQ, D_MODEL), f32)
    meta_tokens = jax.random.normal(next(ks), (N_META, D_MODEL), f32)

    a_c = jax.random.uniform(next(ks), (L, D_LRU), f32, 0.9, 0.999)
    s = a_c ** (1.0 / LRU_C)
    lru_lambda = jnp.log(s) - jnp.log1p(-s)

    return {
        "x": x,
        "meta_tokens": meta_tokens,
        "ffn1_pre_g": gain((L, D_MODEL)),
        "ffn1_w_gate": nrm((L, D_MODEL, D_FF), D_MODEL),
        "ffn1_w_up": nrm((L, D_MODEL, D_FF), D_MODEL),
        "ffn1_w_down": nrm((L, D_FF, D_MODEL), D_FF),
        "ffn1_post_g": gain((L, D_MODEL)),
        "mix_pre_g": gain((L, D_MODEL)),
        "w_in": nrm((L, D_MODEL, IN_COLS), D_MODEL),
        "lru_conv_w": nrm((L, LRU_CONV_WIDTH, D_LRU), LRU_CONV_WIDTH),
        "lru_conv_b": bias((L, D_LRU)),
        "lru_w_a": nrm((L, N_LRU_HEADS, LRU_BLOCK, LRU_BLOCK), LRU_BLOCK),
        "lru_b_a": bias((L, D_LRU)),
        "lru_w_x": nrm((L, N_LRU_HEADS, LRU_BLOCK, LRU_BLOCK), LRU_BLOCK),
        "lru_b_x": bias((L, D_LRU)),
        "lru_lambda": lru_lambda,
        "sconv_w": nrm((L, SCONV_WIDTH, D_SCONV), SCONV_WIDTH),
        "lru_out_g": gain((L, D_LRU)),
        "sconv_out_g": gain((L, D_SCONV)),
        "w_out": nrm((L, D_MODEL, D_MODEL), D_MODEL),
        "mix_post_g": gain((L, D_MODEL)),
        "ffn2_pre_g": gain((L, D_MODEL)),
        "ffn2_w_gate": nrm((L, D_MODEL, D_FF), D_MODEL),
        "ffn2_w_up": nrm((L, D_MODEL, D_FF), D_MODEL),
        "ffn2_w_down": nrm((L, D_FF, D_MODEL), D_FF),
        "ffn2_post_g": gain((L, D_MODEL)),
    }

def reference(x, meta_tokens, ffn1_pre_g, ffn1_w_gate, ffn1_w_up, ffn1_w_down, ffn1_post_g,
              mix_pre_g, w_in, lru_conv_w, lru_conv_b, lru_w_a, lru_b_a, lru_w_x, lru_b_x,
              lru_lambda, sconv_w, lru_out_g, sconv_out_g, w_out, mix_post_g,
              ffn2_pre_g, ffn2_w_gate, ffn2_w_up, ffn2_w_down, ffn2_post_g):
    bn = x.shape[0]
    meta = jnp.broadcast_to(meta_tokens.astype(x.dtype)[None], (bn, N_META, x.shape[-1]))
    h = jnp.concatenate([meta, x], axis=1)
    splits = [D_LRU, 2 * D_LRU, 2 * D_LRU + D_SCONV, 2 * D_LRU + 2 * D_SCONV]

    for l in range(DEPTH):
        f = swiglu(rmsnorm(h, ffn1_pre_g[l]), ffn1_w_gate[l], ffn1_w_up[l], ffn1_w_down[l])
        h = h + 0.5 * rmsnorm(f, ffn1_post_g[l])

        u = rmsnorm(h, mix_pre_g[l])
        z = u @ w_in[l]
        y_lru, x_lru, b_sc, c_sc, v_sc = jnp.split(z, splits, axis=-1)

        x_lru = causal_depthwise_conv(x_lru, lru_conv_w[l]) + lru_conv_b[l]
        lru_out = rg_lru(x_lru, lru_w_a[l], lru_b_a[l], lru_w_x[l], lru_b_x[l], lru_lambda[l])
        lru_out = lru_out * jax.nn.gelu(y_lru, approximate=True)

        sc_out = b_sc * causal_depthwise_conv(c_sc * v_sc, sconv_w[l])

        mixed = jnp.concatenate([
            group_rmsnorm(lru_out, lru_out_g[l], N_LRU_HEADS),
            group_rmsnorm(sc_out, sconv_out_g[l], N_SCONV_GROUPS)], axis=-1)
        h = h + rmsnorm(mixed @ w_out[l], mix_post_g[l])

        f = swiglu(rmsnorm(h, ffn2_pre_g[l]), ffn2_w_gate[l], ffn2_w_up[l], ffn2_w_down[l])
        h = h + 0.5 * rmsnorm(f, ffn2_post_g[l])

    return h[:, N_META:]


_drawn_inputs = setup_inputs


def setup_inputs(seed=0):
    import zlib

    import numpy as np

    out = dict(_drawn_inputs(seed))
    spreads = {}
    factors = {'ffn1_pre_g': 3.208,
     'ffn1_post_g': 4.467,
     'lru_b_a': 32.358,
     'lru_b_x': 23.774,
     'lru_out_g': 24.857,
     'sconv_out_g': 24.209,
     'mix_post_g': 11.487,
     'ffn2_pre_g': 18.35,
     'ffn2_post_g': 34.022}
    for name, (base, spread) in spreads.items():
        noise = np.random.default_rng([zlib.crc32(name.encode()), seed]).standard_normal(out[name].shape)
        drawn = base * np.exp(spread * noise) if base else spread * noise
        out[name] = __import__('jax').numpy.asarray(drawn.astype(out[name].dtype))
    for name, factor in factors.items():
        out[name] = (out[name] * factor).astype(out[name].dtype)
    return out
```

```python
from contextlib import ExitStack

import concourse.bass as bass
from concourse import mybir

ALU = mybir.AluOpType
ACT = mybir.ActivationFunctionType
AX = mybir.AxisListType
F32 = mybir.dt.float32
F32R = mybir.dt.float32r

P = 128
RING = 4
META, SEQ, D = 16, 256, 2048
T = META + SEQ
KT = D // P
FT = 5504 // P
CHUNKS = (16, 16, FT - 32)
CHUNK0 = (0, 16, 32)
UB = 16
LT = 8
HEAD = 64
EPS = 1e-6
GELU_CUBIC = 0.044715
GELU_SIGMOID = 2.0 * 0.7978845608028654
CV0 = META - 2



def ffn_plan(unit, out, hid):
    plan = []
    for nf in CHUNKS:
        plan.append(dict(gu_u=unit, gu_o=out, f0=hid, nf=nf, dn_u=unit + 2 * nf, dn_o=out + 2 * nf))
        unit += 2 * nf + nf * KT // UB
        out += 2 * nf + KT
        hid += nf
    return plan, unit, out, hid


FFN1, IN_U, IN_O, HID1 = ffn_plan(0, 0, 0)
OUT_U, OUT_O = IN_U + 5 * LT, IN_O + 5 * LT
FFN2, UNITS, OUTPUTS, _ = ffn_plan(OUT_U + KT, OUT_O + KT, HID1)
LAST_DOWN = CHUNKS[2]

VEC = {}
_at = 0
for _name, _n in (("ffn1_pre_g", KT), ("ffn1_post_g", KT), ("mix_pre_g", KT), ("mix_post_g", KT),
                  ("ffn2_pre_g", KT), ("ffn2_post_g", KT), ("lru_conv_w", 4 * LT), ("lru_conv_b", LT),
                  ("lru_b_a", LT), ("lru_b_x", LT), ("lru_lambda", LT), ("sconv_w", 3 * LT),
                  ("lru_out_g", LT), ("sconv_out_g", LT)):
    VEC[_name] = _at
    _at += _n
NVEC = _at
DECAY_POS, DECAY_NEG = NVEC, NVEC + LT
SCRATCH = NVEC + 2 * LT
VCOLS = SCRATCH + 4 * LT


def outputs_through(j):
    return -(-UB * (j + 1) // LAST_DOWN)


def hymba_layer_kernel(nc, xt, weights, gates, vectors, out):
    with ExitStack() as ctx:
        at = [16512]

        def sb(name, shape, dt=F32, offset=None):
            size = 4
            for n in shape[1:]:
                size *= n
            if offset is None:
                offset = at[0]
                at[0] += -(-size // 32) * 32
            return nc.alloc_sbuf_tensor_at(name, shape, dt, offset=offset)

        def sem(name):
            return ctx.enter_context(nc.semaphore(name))

        raw = sb("raw", [P, RING, UB * P])
        w_hi = sb("w_hi", [P, RING, UB * P], F32R)
        w_lo = sb("w_lo", [P, RING, UB * P], F32R)
        h = sb("h", [P, KT, T])
        x_hi = sb("x_hi", [P, KT, T], F32R)
        x_lo = sb("x_lo", [P, KT, T], F32R)
        hid_hi = sb("hid_hi", [P, CHUNKS[0], T], F32R)
        hid_lo = sb("hid_lo", [P, CHUNKS[0], T], F32R)
        facc_at = at[0]
        facc = sb("facc", [P, KT, T])
        rms = sb("rms", [P, T])
        ssum = sb("ssum", [P, T])
        sq = sb("sq", [P, T])
        tg = sb("tg", [P, T])
        tu = sb("tu", [P, T])
        ones = sb("ones", [P, P])
        head_ones = sb("head_ones", [P, P])
        vec = sb("vec", [P, VCOLS])
        zx = sb("zx", [P, 3 + T])
        gate_diag = sb("gate_diag", [P, 2, P])
        assert at[0] <= 229344, at[0]

        mat = [facc_at]

        def over(name, shape):
            size = 4
            for n in shape[1:]:
                size *= n
            t = sb(name, shape, F32, offset=mat[0])
            mat[0] += -(-size // 32) * 32
            return t

        gate_w = over("gate_w", [P, 2, LT, HEAD])
        xc = over("xc", [P, T])
        yz = over("yz", [P, SEQ])
        y3 = over("y3", [P, SEQ])
        bz = over("bz", [P, SEQ])
        cz = over("cz", [P, T - CV0])
        cv = over("cv", [P, T - CV0])
        decay = over("decay", [P, T])
        inject = over("inject", [P, T])
        o_lru = over("o_lru", [P, SEQ])
        o_sc = over("o_sc", [P, SEQ])
        head_sq = over("head_sq", [P, 2, SEQ])
        assert mat[0] <= facc_at + 4 * KT * T, mat[0] - facc_at
        gx, scan, gy = tu, tg, sq

        bank = [nc.alloc_psum_tensor(f"bank{n}", [P, 512], F32) for n in range(8)]
        GATE_A, GATE_X, HEAD_SUM, TOKEN_SUM = bank[4], bank[5], bank[6], bank[7]

        raw_in = [sem(f"raw_in{n}") for n in range(RING)]
        w_hi_done = sem("w_hi_done")
        w_lo_done = sem("w_lo_done")
        out_done = sem("out_done")
        out_taken = sem("out_taken")
        x_in = [sem(f"x_in{n}") for n in range(4)]
        vec_in = sem("vec_in")
        gate_w_in = sem("gate_w_in")
        consts_set = sem("consts_set")
        h_ready = sem("h_ready")
        x_hi_done = sem("x_hi_done")
        x_lo_done = sem("x_lo_done")
        h_sq_done = sem("h_sq_done")
        ssum_ready = sem("ssum_ready")
        token_sum_done = sem("token_sum_done")
        recip_ready = sem("recip_ready")
        rms_ready = sem("rms_ready")
        silu_done = sem("silu_done")
        hidden_ready = sem("hidden_ready")
        hid_hi_done = sem("hid_hi_done")
        hid_lo_done = sem("hid_lo_done")
        sq_done = sem("sq_done")
        sq_added = sem("sq_added")
        tap0_done = sem("tap0_done")
        xc_ready = sem("xc_ready")
        y_sq_done = sem("y_sq_done")
        y3_ready = sem("y3_ready")
        gelu_gate_done = sem("gelu_gate_done")
        gate_diag_ready = sem("gate_diag_ready")
        gates_done = sem("gates_done")
        decay_ready = sem("decay_ready")
        inject_sq_ready = sem("inject_sq_ready")
        inject_ready = sem("inject_ready")
        lru_out_ready = sem("lru_out_ready")
        sc_out_ready = sem("sc_out_ready")
        head_sq_done = sem("head_sq_done")
        head_sum_done = sem("head_sum_done")
        head_recip_ready = sem("head_recip_ready")
        head_rms_ready = sem("head_rms_ready")
        mixed_ready = sem("mixed_ready")
        mixed_hi_done = sem("mixed_hi_done")
        mixed_lo_done = sem("mixed_lo_done")
        act_order = sem("act_order")
        dve_order = sem("dve_order")
        exp_lambda_done = sem("exp_lambda_done")
        lambda_abs_ready = sem("lambda_abs_ready")
        decay_rate_ready = sem("decay_rate_ready")
        out_ready = sem("out_ready")
        stored = sem("stored")

        def col(name, k=0):
            c = (VEC[name] if isinstance(name, str) else name) + k
            return vec[:, bass.ds(c, 1)] if not isinstance(c, int) else vec[:, c:c + 1]

        def psum(o, n):
            return bank[o % RING][:, 0:n]

        def tile_of(buf, k, c0=0, c1=T):
            if isinstance(k, int):
                return buf[:, k, c0:c1]
            return buf[:, bass.ds(k, 1), c0:c1].rearrange("p a t -> p (a t)")

        block = ctx.enter_context(nc.Block())

        @block.sync
        def _(sp):
            def load_unit(v, slot):
                sp.dma_start(raw[:, slot], weights[v]).then_inc(raw_in[slot], 16)

            for v in range(RING):
                load_unit(v, v)
            loops = (UNITS - RING) // RING
            with sp.Fori(0, loops) as i:
                for j in range(RING):
                    sp.wait_ge(w_lo_done, i * RING + (j + 1))
                    src = weights[bass.ds(i * RING + (RING + j), 1)].rearrange("a p n -> (a p) n")
                    sp.dma_start(raw[:, j], src).then_inc(raw_in[j], 16)
            for v in range(RING + loops * RING, UNITS):
                sp.wait_ge(w_lo_done, v - RING + 1)
                load_unit(v, v % RING)
            for g in range(4):
                sp.wait_ge(out_ready, g + 1)
                sp.dma_start(out[:, 4 * g:4 * g + 4, :], facc[:, 4 * g:4 * g + 4, META:T]).then_inc(stored, 16)
            sp.wait_ge(stored, 64)

        @block.gpsimd
        def _(pool):
            pool.memset(ones[:], 1.0)
            pool.memset(zx[:, 0:3], 0.0)
            pool.memset(gate_diag[:], 0.0)
            pool.memset(head_ones[:], 0.0).then_inc(consts_set, 1)
            pool.wait_ge(consts_set, 1)
            pool.memset(head_ones[0:HEAD, 0:HEAD], 1.0)
            pool.memset(head_ones[HEAD:P, HEAD:P], 1.0).then_inc(consts_set, 1)
            pool.wait_ge(ssum_ready, 3)
            pool.dma_start(gate_w[:], gates).then_inc(gate_w_in, 16)
            pool.wait_ge(gate_w_in, 16)
            for t in range(LT):
                if t:
                    pool.wait_ge(gates_done, t)
                pool.tensor_copy(gate_diag[0:HEAD, :, 0:HEAD], gate_w[0:HEAD, :, t, :])
                pool.tensor_copy(gate_diag[HEAD:P, :, HEAD:P], gate_w[HEAD:P, :, t, :]).then_inc(gate_diag_ready, 1)

        @block.tensor
        def _(pe):
            def three(o, slot, b, mov_hi, mov_lo, first, last):
                hi, lo = w_hi[:, slot, b * P:(b + 1) * P], w_lo[:, slot, b * P:(b + 1) * P]
                acc = psum(o, mov_hi.shape[-1])
                pe.matmul(acc, hi, mov_hi, start=first, stop=False)
                pe.matmul(acc, hi, mov_lo, start=False, stop=False)
                mm = pe.matmul(acc, lo, mov_hi, start=False, stop=last)
                if last:
                    mm.then_inc(out_done, 1)

            def unit_ready(u, i=0):
                pe.wait_ge(w_lo_done, i * RING + (u + 1))

            def bank_free(o, i=0):
                if not isinstance(i, int) or o >= RING:
                    pe.wait_ge(out_taken, i * RING + (o - RING + 1))

            def unit(u, o, hi, lo, c0, c1, i=0, ready=()):
                unit_ready(u, i)
                bank_free(o, i)
                for k in range(UB):
                    if k in ready:
                        pe.wait_ge(*ready[k])
                    three(o, u % RING, k, hi[:, k, c0:c1], lo[:, k, c0:c1], k == 0, k == UB - 1)

            def first_four(u, o, hi, lo, cols, ready, order=range(UB), after=None):
                order, together = list(order), 12
                for s in range(RING):
                    unit_ready(u + s)
                    bank_free(o + s)
                steps = [(s, n) for n in range(together) for s in range(RING)]
                steps += [(s, n) for s in range(RING) for n in range(together, UB)]
                for at, (s, n) in enumerate(steps):
                    k, (c0, c1) = order[n], cols[s]
                    if s == 0 and k in ready:
                        pe.wait_ge(*ready[k])
                    three(o + s, (u + s) % RING, k, hi[:, k, c0:c1], lo[:, k, c0:c1], n == 0, n == UB - 1)
                    if after and at == after[0]:
                        after[1]()

            def token_sum(count, c0):
                pe.wait_ge(ssum_ready, count)
                pe.matmul(TOKEN_SUM[:, c0:T], ones[:], ssum[:, c0:T], start=True, stop=True).then_inc(token_sum_done, 1)

            def operand_tiles(first):
                return {k: (x_lo_done, first + k + 1) for k in range(KT)}

            def ffn(plan, c0, operand, sums):
                n = T - c0
                for c, q in enumerate(plan):
                    u, o, units = q["gu_u"], q["gu_o"], 2 * q["nf"]
                    if c == 0:
                        if u == 0:
                            unit(0, 0, x_hi, x_lo, c0, T, ready=operand_tiles(operand))
                            unit(1, 1, x_hi, x_lo, c0, T)
                            token_sum(sums, c0)
                            unit(2, 2, x_hi, x_lo, c0, T)
                            unit(3, 3, x_hi, x_lo, c0, T)
                        else:
                            first_four(u, o, x_hi, x_lo, [(c0, T)] * RING, operand_tiles(operand))
                            token_sum(sums, c0)
                        u, o, units = u + RING, o + RING, units - RING
                    with pe.Fori(0, units // RING) as i:
                        for j in range(RING):
                            unit(u + j, o + j, x_hi, x_lo, c0, T, i)
                    for j in range(units - units % RING, units):
                        unit(u + j, o + j, x_hi, x_lo, c0, T)
                    u, o, nf = q["dn_u"], q["dn_o"], q["nf"]
                    late = {k: (hid_lo_done, q["f0"] + k + 1) for k in (nf - 3, nf - 2, nf - 1)}
                    if nf == UB:
                        with pe.Fori(0, KT // RING) as i:
                            for j in range(RING):
                                unit(u + j, o + j, hid_hi, hid_lo, 0, n, i, late if j == 0 else ())
                    else:
                        for m in range(KT):
                            bank_free(o + m)
                            for k in range(nf):
                                b = m * nf + k
                                if b % UB == 0:
                                    unit_ready(u + b // UB)
                                if m == 0 and k in late:
                                    pe.wait_ge(*late[k])
                                three(o + m, (u + b // UB) % RING, b % UB, hid_hi[:, k, 0:n], hid_lo[:, k, 0:n],
                                      k == 0, k == nf - 1)
                token_sum(sums + 1, c0)

            def head_products(t):
                pe.wait_ge(xc_ready, t + 1)
                pe.wait_ge(gate_diag_ready, t + 1)
                pe.matmul(GATE_A[:, 0:T], gate_diag[:, 0, :], xc[:], start=True, stop=True)
                pe.matmul(GATE_X[:, 0:T], gate_diag[:, 1, :], xc[:], start=True, stop=True).then_inc(gates_done, 1)

            def head_sums(t):
                pe.wait_ge(head_sq_done, t + 1)
                pe.matmul(HEAD_SUM[:, :], head_ones[:], head_sq[:].rearrange("p a t -> p (a t)"),
                          start=True, stop=True).then_inc(head_sum_done, 1)

            pe.wait_ge(consts_set, 2)
            ffn(FFN1, 0, 0, 1)

            cols = [(0, T), (META, T), (META, T), (CV0, T), (CV0, T)]
            first_four(IN_U, IN_O, x_hi, x_lo, cols, operand_tiles(KT))
            token_sum(3, 0)
            head_products(0)
            unit(IN_U + 4, IN_O + 4, x_hi, x_lo, *cols[4])
            for t in range(1, LT):
                u, o = IN_U + 5 * t, IN_O + 5 * t
                for z in range(3):
                    unit(u + z, o + z, x_hi, x_lo, *cols[z])
                head_products(t)
                head_sums(t - 1)
                for z in range(3, 5):
                    unit(u + z, o + z, x_hi, x_lo, *cols[z])

            order = [*range(LT - 1), *range(LT, 2 * LT - 1), LT - 1, 2 * LT - 1]
            first_four(OUT_U, OUT_O, hid_hi, hid_lo, [(META, T)] * RING,
                       {0: (mixed_lo_done, LT - 1), LT - 1: (mixed_lo_done, LT)}, order,
                       after=(11, lambda: head_sums(LT - 1)))
            with pe.Fori(0, KT // RING - 1) as i:
                for j in range(RING):
                    unit(OUT_U + RING + j, OUT_O + RING + j, hid_hi, hid_lo, META, T, i)
            token_sum(4, META)

            ffn(FFN2, META, 2 * KT, 5)

        @block.scalar
        def _(act):
            links = [0]

            def link(instruction):
                links[0] += 1
                instruction.then_inc(act_order, 1)
                act.wait_ge(act_order, links[0])

            def split_head(v, used, i=0):
                slot = v % RING
                act.wait_ge(raw_in[slot], i * 16 + 16 * (v // RING + 1))
                if used:
                    act.wait_ge(out_done, i * RING + used)
                act.activation(w_hi[:, slot], raw[:, slot], ACT.Copy).then_inc(w_hi_done, 1)

            def root(count, c0):
                act.wait_ge(recip_ready, count)
                act.activation(rms[:, c0:T], rms[:, c0:T], ACT.Sqrt).then_inc(rms_ready, 1)

            def operand_heads(gain, c0, renewed):
                for k in range(KT):
                    if renewed is None:
                        act.wait_ge(x_in[k // 4], 16)
                    else:
                        act.wait_ge(h_ready, renewed + k + 1)
                    act.activation(x_hi[:, k, c0:T], h[:, k, c0:T], ACT.Copy, scale=col(gain, k)).then_inc(x_hi_done, 1)
                    act.activation(facc[:, k, c0:T], h[:, k, c0:T], ACT.Square).then_inc(h_sq_done, 1)

            def gate_up(u, o, f, n, split=(True, True), i=0):
                fi = f if isinstance(i, int) else i * 2 + f
                if split[0]:
                    split_head(u + RING, o + 1, i)
                act.wait_ge(out_taken, i * RING + (o + 1))
                act.activation(sq[:, 0:n], tg[:, 0:n], ACT.Silu).then_inc(silu_done, 1)
                if split[1]:
                    split_head(u + 1 + RING, o + 2, i)
                act.wait_ge(hidden_ready, fi + 1)
                return fi

            def hidden_head(k, n):
                act.activation(tile_of(hid_hi, k, 0, n), tu[:, 0:n], ACT.Copy).then_inc(hid_hi_done, 1)

            def square_output(k, c0, first, i=0):
                act.wait_ge(sq_added, i * RING + (first + 1))
                act.activation(sq[:, c0:T], tile_of(facc, k, c0), ACT.Square).then_inc(sq_done, 1)

            def ffn(plan, c0, squares):
                n = T - c0
                for q in plan:
                    u, o, f0, nf = q["gu_u"], q["gu_o"], q["f0"], q["nf"]
                    act.preload_act_table(ACT.Silu)
                    with act.Fori(0, nf // 2) as i:
                        for j in range(2):
                            gate_up(u + 2 * j, o + 2 * j, f0 + j, n, i=i)
                            hidden_head(i * 2 + j, n)
                    if nf % 2:
                        gate_up(u + 2 * nf - 2, o + 2 * nf - 2, f0 + nf - 1, n)
                        hidden_head(nf - 1, n)
                    u, o = q["dn_u"], q["dn_o"]
                    if nf == UB:
                        with act.Fori(0, KT // RING) as i:
                            for j in range(RING):
                                split_head(u + j + RING, o + j + 1, i)
                        continue
                    m = 0
                    for j in range(nf):
                        done = outputs_through(j)
                        if u + j + RING < UNITS:
                            split_head(u + j + RING, o + done)
                        while m < done:
                            square_output(m, c0, squares + m)
                            m += 1

            act.dma_start(vec[:, 0:NVEC], vectors).then_inc(vec_in, 16)
            for g in range(4):
                act.dma_start(h[:, 4 * g:4 * g + 4, :], xt[:, 4 * g:4 * g + 4, :]).then_inc(x_in[g], 16)
            act.wait_ge(vec_in, 16)
            split_head(0, 0)
            operand_heads("ffn1_pre_g", 0, None)
            split_head(1, 0)
            split_head(2, 0)
            root(1, 0)
            split_head(3, 0)
            act.wait_ge(lambda_abs_ready, 1)
            act.activation(vec[:, SCRATCH:SCRATCH + LT], vec[:, SCRATCH:SCRATCH + LT], ACT.Exp,
                           scale=-1.0).then_inc(exp_lambda_done, 1)
            ffn(FFN1, 0, 0)
            root(2, 0)
            operand_heads("mix_pre_g", 0, 0)
            root(3, 0)

            def square_lru(t):
                act.wait_ge(lru_out_ready, t + 1)
                act.activation(head_sq[:, 0, :], o_lru[:], ACT.Square).then_inc(head_sq_done, 1)

            def head_root(t):
                act.wait_ge(head_recip_ready, t + 1)
                act.activation(head_sq[:], head_sq[:], ACT.Sqrt).then_inc(head_rms_ready, 1)

            def mixed_heads(t):
                act.wait_ge(mixed_ready, t + 1)
                act.activation(hid_hi[:, t, META:T], o_lru[:], ACT.Copy, scale=col("lru_out_g", t))
                act.activation(hid_hi[:, LT + t, META:T], o_sc[:], ACT.Copy,
                               scale=col("sconv_out_g", t)).then_inc(mixed_hi_done, 1)

            act.wait_ge(decay_rate_ready, 1)
            for t in range(LT):
                u, o = IN_U + 5 * t, IN_O + 5 * t
                split_head(u + RING, o + 1)
                act.wait_ge(out_taken, o + 1)
                act.activation(xc[:], zx[:, 0:T], ACT.Identity, bias=col("lru_conv_b", t),
                               scale=col("lru_conv_w", t)).then_inc(tap0_done, 1)
                if t:
                    square_lru(t - 1)
                split_head(u + 1 + RING, o + 2)
                act.wait_ge(out_taken, o + 2)
                act.activation(y3[:], yz[:], ACT.Square).then_inc(y_sq_done, 1)
                split_head(u + 2 + RING, o + 3)
                act.wait_ge(y3_ready, t + 1)
                act.activation(gy[:, 0:SEQ], y3[:], ACT.Sigmoid, scale=GELU_SIGMOID).then_inc(gelu_gate_done, 1)
                split_head(u + 3 + RING, o + 4)
                act.wait_ge(gates_done, t + 1)
                act.activation(gx[:], GATE_X[:, 0:T], ACT.Sigmoid, bias=col("lru_b_x", t))
                link(act.activation(decay[:], GATE_A[:, 0:T], ACT.Sigmoid, bias=col("lru_b_a", t)))
                link(act.activation(inject[:], decay[:], ACT.Tanh, scale=col(DECAY_POS, t)))
                link(act.activation(decay[:], decay[:], ACT.Exp, scale=col(DECAY_NEG, t)))
                act.activation(scan[:], decay[:], ACT.Square).then_inc(decay_ready, 1)
                if t:
                    head_root(t - 1)
                act.wait_ge(inject_sq_ready, t + 1)
                act.activation(inject[:], inject[:], ACT.Sqrt).then_inc(inject_ready, 1)
                split_head(u + 4 + RING, o + 5)
                if t:
                    mixed_heads(t - 1)
                act.wait_ge(sc_out_ready, t + 1)
                act.activation(head_sq[:, 1, :], o_sc[:], ACT.Square)
            square_lru(LT - 1)
            head_root(LT - 1)
            mixed_heads(LT - 1)

            with act.Fori(0, KT // RING) as i:
                for j in range(RING):
                    split_head(OUT_U + j + RING, OUT_O + j + 1, i)
                    square_output(i * RING + j, META, KT + j, i)
            root(4, META)
            operand_heads("ffn2_pre_g", META, KT)
            root(5, META)
            ffn(FFN2, META, 2 * KT)
            root(6, META)

        @block.vector
        def _(dve):
            links = [0]

            def link(instruction):
                links[0] += 1
                instruction.then_inc(dve_order, 1)
                dve.wait_ge(dve_order, links[0])

            def split_rest(v, i=0):
                slot = v % RING
                dve.wait_ge(w_hi_done, i * RING + (v + 1))
                dve.tensor_tensor(w_lo[:, slot], raw[:, slot], w_hi[:, slot].bitcast(F32),
                                  ALU.subtract).then_inc(w_lo_done, 1)

            def operand_rest(k, gain, c0, first):
                dve.wait_ge(x_hi_done, first + k + 1)
                dve.scalar_tensor_tensor(x_lo[:, k, c0:T], h[:, k, c0:T], col(gain, k), x_hi[:, k, c0:T].bitcast(F32),
                                         ALU.mult, ALU.subtract).then_inc(x_lo_done, 1)

            def sum_h_squares(c0, first):
                dve.wait_ge(h_sq_done, first + KT)
                dve.tensor_reduce(ssum[:, c0:T], facc[:, :, c0:T].rearrange("p k t -> p t k"), AX.X,
                                  ALU.add).then_inc(ssum_ready, 1)

            def token_rms(count, c0):
                dve.wait_ge(token_sum_done, count)
                link(dve.tensor_scalar(ssum[:, c0:T], TOKEN_SUM[:, c0:T], 1.0 / D, EPS, ALU.mult, ALU.add))
                dve.reciprocal(rms[:, c0:T], ssum[:, c0:T]).then_inc(recip_ready, 1)

            def new_residual(post, pre, c0, first, lo_first):
                for k in range(KT):
                    link(dve.tensor_tensor(facc[:, k, c0:T], facc[:, k, c0:T], rms[:, c0:T], ALU.mult))
                    dve.scalar_tensor_tensor(h[:, k, c0:T], facc[:, k, c0:T], col(post, k), h[:, k, c0:T],
                                             ALU.mult, ALU.add).then_inc(h_ready, 1)
                    if k:
                        operand_rest(k - 1, pre, c0, lo_first)
                operand_rest(KT - 1, pre, c0, lo_first)

            def add_square(count, c0, last=False, i=0):
                dve.wait_ge(sq_done, i * RING + count)
                dve.tensor_tensor(ssum[:, c0:T], ssum[:, c0:T], sq[:, c0:T], ALU.add).then_inc(
                    ssum_ready if last else sq_added, 1)

            def clear_sum(c0):
                dve.memset(ssum[:, c0:T], 0.0).then_inc(sq_added, 1)

            def gate_up(u, o, f, k, n, split=(True, True), i=0):
                fi = f if isinstance(i, int) else i * 2 + f
                c0 = T - n
                dve.wait_ge(out_done, i * RING + (o + 1))
                dve.tensor_tensor(tg[:, 0:n], psum(o, n), rms[:, c0:T], ALU.mult).then_inc(out_taken, 1)
                if split[0]:
                    split_rest(u + RING, i)
                dve.wait_ge(out_done, i * RING + (o + 2))
                dve.wait_ge(w_lo_done, i * RING + (u + RING + 1 if split[0] else u + RING))
                dve.tensor_tensor(tu[:, 0:n], psum(o + 1, n), rms[:, c0:T], ALU.mult).then_inc(out_taken, 1)
                dve.wait_ge(out_taken, i * RING + (o + 2))
                dve.wait_ge(silu_done, fi + 1)
                dve.tensor_tensor(tu[:, 0:n], tu[:, 0:n], sq[:, 0:n], ALU.mult).then_inc(hidden_ready, 1)
                if split[1]:
                    split_rest(u + 1 + RING, i)
                dve.wait_ge(hid_hi_done, fi + 1)
                dve.tensor_tensor(tile_of(hid_lo, k, 0, n), tu[:, 0:n], tile_of(hid_hi, k, 0, n).bitcast(F32),
                                  ALU.subtract).then_inc(hid_lo_done, 1)

            def ffn(plan, c0, squares):
                n = T - c0
                for c, q in enumerate(plan):
                    u, o, f0, nf = q["gu_u"], q["gu_o"], q["f0"], q["nf"]
                    with dve.Fori(0, nf // 2) as i:
                        for j in range(2):
                            gate_up(u + 2 * j, o + 2 * j, f0 + j, i * 2 + j, n, i=i)
                    if nf % 2:
                        gate_up(u + 2 * nf - 2, o + 2 * nf - 2, f0 + nf - 1, nf - 1, n)
                    u, o = q["dn_u"], q["dn_o"]

                    def down(m, at, i=0):
                        dve.wait_ge(out_done, i * RING + (at + 1))
                        f = tile_of(facc, m, c0)
                        if c == 0:
                            dve.tensor_copy(f, psum(at, n)).then_inc(out_taken, 1)
                        else:
                            dve.tensor_tensor(f, psum(at, n), f, ALU.add).then_inc(out_taken, 1)

                    if nf == UB:
                        with dve.Fori(0, KT // RING) as i:
                            for j in range(RING):
                                down(i * RING + j, o + j, i)
                                split_rest(u + j + RING, i)
                        continue
                    m = 0
                    for j in range(nf):
                        done = outputs_through(j)
                        while m < done:
                            down(m, o + m)
                            dve.wait_ge(out_taken, o + m + 1)
                            if m == 0:
                                clear_sum(c0)
                            else:
                                add_square(squares + m, c0)
                            m += 1
                        if u + j + RING < UNITS:
                            split_rest(u + j + RING)
                add_square(squares + KT, c0, last=True)

            split_rest(0)
            for k in range(KT):
                operand_rest(k, "ffn1_pre_g", 0, 0)
            split_rest(1)
            sum_h_squares(0, 0)
            split_rest(2)
            token_rms(1, 0)
            split_rest(3)

            for name in ("ffn1_post_g", "ffn2_post_g"):
                g = vec[:, VEC[name]:VEC[name] + KT]
                link(dve.tensor_scalar(g, g, 0.5, None, ALU.mult))
            lam = vec[:, VEC["lru_lambda"]:VEC["lru_lambda"] + LT]
            e, s, s2, poly = (vec[:, SCRATCH + n * LT:SCRATCH + (n + 1) * LT] for n in range(4))
            rate, minus = vec[:, DECAY_POS:DECAY_POS + LT], vec[:, DECAY_NEG:DECAY_NEG + LT]
            link(dve.tensor_scalar(minus, lam, -1.0, 0.0, ALU.mult, ALU.max))
            link(dve.tensor_scalar(rate, lam, 0.0, None, ALU.max))
            dve.tensor_tensor(e, rate, minus, ALU.add).then_inc(lambda_abs_ready, 1)
            dve.wait_ge(exp_lambda_done, 1)
            link(dve.tensor_scalar(s2, e, 2.0, None, ALU.add))
            link(dve.reciprocal(s, s2))
            link(dve.tensor_tensor(s, s, e, ALU.mult))
            link(dve.tensor_tensor(s2, s, s, ALU.mult))
            link(dve.tensor_scalar(poly, s2, 2.0 / 17, 2.0 / 15, ALU.mult, ALU.add))
            for n in (13, 11, 9, 7, 5, 3, 1):
                link(dve.tensor_tensor(poly, poly, s2, ALU.mult))
                link(dve.tensor_scalar(poly, poly, 2.0 / n, None, ALU.add))
            link(dve.tensor_tensor(poly, poly, s, ALU.mult))
            link(dve.tensor_tensor(poly, poly, minus, ALU.add))
            link(dve.tensor_scalar(rate, poly, 8.0, None, ALU.mult))
            dve.tensor_scalar(minus, poly, -8.0, None, ALU.mult).then_inc(decay_rate_ready, 1)

            dve.wait_ge(rms_ready, 1)
            ffn(FFN1, 0, 0)
            token_rms(2, 0)
            dve.wait_ge(rms_ready, 2)
            new_residual("ffn1_post_g", "mix_pre_g", 0, 0, KT)
            sum_h_squares(0, KT)
            token_rms(3, 0)
            dve.wait_ge(rms_ready, 3)
            rms_sq = ssum
            link(dve.tensor_tensor(rms_sq[:], rms[:], rms[:], ALU.mult))

            def take(o, buf, c0, by):
                dve.wait_ge(out_done, o + 1)
                dve.tensor_tensor(buf, psum(o, T - c0), by[:, c0:T], ALU.mult).then_inc(out_taken, 1)

            def recurrence(t):
                dve.wait_ge(inject_ready, t + 1)
                link(dve.tensor_tensor(gx[:], gx[:], inject[:], ALU.mult))
                link(dve.tensor_tensor_scan(scan[:], decay[:], gx[:], 0.0, ALU.mult, ALU.add))
                dve.tensor_tensor(o_lru[:], scan[:, META:T], gy[:, 0:SEQ], ALU.mult).then_inc(lru_out_ready, 1)

            def head_recip(t):
                dve.wait_ge(head_sum_done, t + 1)
                both = head_sq[:].rearrange("p a t -> p (a t)")
                link(dve.tensor_scalar(both, HEAD_SUM[:, :], 1.0 / HEAD, EPS, ALU.mult, ALU.add))
                dve.reciprocal(both, both).then_inc(head_recip_ready, 1)

            def normed(t):
                dve.wait_ge(head_rms_ready, t + 1)
                dve.tensor_tensor(o_lru[:], o_lru[:], head_sq[:, 0, :], ALU.mult)
                dve.tensor_tensor(o_sc[:], o_sc[:], head_sq[:, 1, :], ALU.mult).then_inc(mixed_ready, 1)

            def mixed_rests(t):
                dve.wait_ge(mixed_hi_done, t + 1)
                dve.scalar_tensor_tensor(hid_lo[:, t, META:T], o_lru[:], col("lru_out_g", t),
                                         hid_hi[:, t, META:T].bitcast(F32), ALU.mult, ALU.subtract)
                dve.scalar_tensor_tensor(hid_lo[:, LT + t, META:T], o_sc[:], col("sconv_out_g", t),
                                         hid_hi[:, LT + t, META:T].bitcast(F32), ALU.mult,
                                         ALU.subtract).then_inc(mixed_lo_done, 1)

            for t in range(LT):
                u, o = IN_U + 5 * t, IN_O + 5 * t
                take(o, zx[:, 3:3 + T], 0, rms)
                if t:
                    recurrence(t - 1)
                split_rest(u + RING)
                take(o + 1, yz[:], META, rms)
                dve.wait_ge(tap0_done, t + 1)
                for w in range(1, 4):
                    tap = dve.scalar_tensor_tensor(xc[:], zx[:, w:w + T], col("lru_conv_w", w * LT + t), xc[:],
                                                   ALU.mult, ALU.add)
                    if w < 3:
                        link(tap)
                tap.then_inc(xc_ready, 1)
                split_rest(u + 1 + RING)
                take(o + 2, bz[:], META, rms)
                dve.wait_ge(y_sq_done, t + 1)
                link(dve.tensor_scalar(y3[:], y3[:], GELU_CUBIC, 1.0, ALU.mult, ALU.add))
                dve.tensor_tensor(y3[:], y3[:], yz[:], ALU.mult).then_inc(y3_ready, 1)
                split_rest(u + 2 + RING)
                take(o + 3, cz[:], CV0, rms_sq)
                dve.wait_ge(gelu_gate_done, t + 1)
                dve.tensor_tensor(gy[:, 0:SEQ], gy[:, 0:SEQ], yz[:], ALU.mult)
                if t:
                    head_recip(t - 1)
                split_rest(u + 3 + RING)
                dve.wait_ge(decay_ready, t + 1)
                dve.tensor_tensor(gx[:], gx[:], xc[:], ALU.mult)
                dve.scalar_tensor_tensor(inject[:], scan[:], 1.0, inject[:], ALU.add,
                                         ALU.mult).then_inc(inject_sq_ready, 1)
                if t:
                    normed(t - 1)
                dve.wait_ge(out_done, o + 5)
                dve.wait_ge(out_taken, o + 4)
                dve.tensor_tensor(cv[:], psum(o + 4, T - CV0), cz[:], ALU.mult).then_inc(out_taken, 1)
                split_rest(u + 4 + RING)
                if t:
                    mixed_rests(t - 1)
                dve.wait_ge(out_taken, o + 5)
                if t:
                    dve.wait_ge(mixed_lo_done, t)
                link(dve.tensor_scalar(o_sc[:], cv[:, 0:SEQ], col("sconv_w", t), None, ALU.mult))
                for w in (1, 2):
                    link(dve.scalar_tensor_tensor(o_sc[:], cv[:, w:w + SEQ], col("sconv_w", w * LT + t), o_sc[:],
                                                  ALU.mult, ALU.add))
                dve.tensor_tensor(o_sc[:], o_sc[:], bz[:], ALU.mult).then_inc(sc_out_ready, 1)
            recurrence(LT - 1)
            head_recip(LT - 1)
            normed(LT - 1)
            mixed_rests(LT - 1)

            def out_tile(m, j, i=0):
                at = OUT_O + j
                dve.wait_ge(out_done, i * RING + (at + 1))
                dve.tensor_copy(tile_of(facc, m, META), psum(at, SEQ)).then_inc(out_taken, 1)
                dve.wait_ge(out_taken, i * RING + (at + 1))

            for j in range(RING):
                out_tile(j, j)
                if j == 0:
                    clear_sum(META)
                else:
                    add_square(KT + j, META)
                split_rest(OUT_U + j + RING)
            with dve.Fori(0, KT // RING - 1) as i:
                for j in range(RING, 2 * RING):
                    out_tile(i * RING + j, j, i)
                    add_square(KT + j, META, i=i)
                    split_rest(OUT_U + j + RING, i)
            add_square(2 * KT, META, last=True)
            token_rms(4, META)
            dve.wait_ge(rms_ready, 4)
            new_residual("mix_post_g", "ffn2_pre_g", META, KT, 2 * KT)
            sum_h_squares(META, 2 * KT)
            token_rms(5, META)
            dve.wait_ge(rms_ready, 5)
            ffn(FFN2, META, 2 * KT)
            token_rms(6, META)
            dve.wait_ge(rms_ready, 6)
            for g in range(4):
                f = facc[:, 4 * g:4 * g + 4, META:T]
                r = rms[:, META:T].rearrange("p (a t) -> p a t", a=1).to_broadcast([P, 4, SEQ])
                link(dve.tensor_tensor(f, f, r, ALU.mult))
                for k in range(4 * g, 4 * g + 4):
                    last = dve.scalar_tensor_tensor(facc[:, k, META:T], facc[:, k, META:T], col("ffn2_post_g", k),
                                                    h[:, k, META:T], ALU.mult, ALU.add)
                last.then_inc(out_ready, 1)


def _tiles(v, n):
    return v.reshape(-1, n, P).transpose(2, 0, 1).reshape(P, -1)


def _by_output(w):
    n = w.shape[1] // P
    return w.reshape(-1, P, n, P).transpose(2, 1, 0, 3).reshape(n, P, -1)


def _ffn_units(np, gate, up, down):
    gu = np.stack([_by_output(gate), _by_output(up)], 1).reshape(2 * FT, P, UB * P)
    units = []
    for f0, nf in zip(CHUNK0, CHUNKS):
        units.append(gu[2 * f0:2 * (f0 + nf)])
        d = _by_output(down[f0 * P:(f0 + nf) * P]).reshape(KT, P, nf, P)
        units.append(d.transpose(0, 2, 1, 3).reshape(nf, UB, P, P).transpose(0, 2, 1, 3).reshape(nf, P, UB * P))
    return units


def kernel(**inputs):
    import numpy as np
    import concourse.bacc as bacc
    from concourse.bass_utils import run_bass_kernel_spmd

    a = {k: np.asarray(v) for k, v in inputs.items()}
    one = {k: v[0] for k, v in a.items() if k != "meta_tokens"}
    tokens = np.concatenate([a["meta_tokens"], one["x"]], 0)
    xt = tokens.T.reshape(KT, P, T).transpose(1, 0, 2)
    w_in = _by_output(one["w_in"]).reshape(5, LT, P, UB * P)[[1, 0, 2, 3, 4]].transpose(1, 0, 2, 3)
    weights = np.concatenate(
        _ffn_units(np, one["ffn1_w_gate"], one["ffn1_w_up"], one["ffn1_w_down"])
        + [w_in.reshape(5 * LT, P, UB * P), _by_output(one["w_out"])]
        + _ffn_units(np, one["ffn2_w_gate"], one["ffn2_w_up"], one["ffn2_w_down"]), 0)
    gates = np.stack([one["lru_w_a"], one["lru_w_x"]]).reshape(2, LT, P, HEAD).transpose(2, 0, 1, 3)
    vectors = np.concatenate([_tiles(one[k], one[k].shape[-1] // P) for k in VEC], 1)
    arrays = {"xt": xt, "weights": weights, "gates": gates, "vectors": vectors}
    arrays = {k: np.ascontiguousarray(v) for k, v in arrays.items()}

    nc = bacc.Bacc("TRN2", target_bir_lowering=False, num_devices=1)
    ins = [nc.dram_tensor(k, v.shape, mybir.dt.from_np(v.dtype), kind="ExternalInput").ap() for k, v in arrays.items()]
    out = nc.dram_tensor("out", (P, KT, SEQ), F32, kind="ExternalOutput").ap()
    hymba_layer_kernel(nc, *ins, out)
    got = run_bass_kernel_spmd(nc, [arrays], core_ids=[0]).results[0]["out"]
    return np.ascontiguousarray(got.transpose(2, 1, 0).reshape(1, SEQ, D))
```

```python
from contextlib import ExitStack

import concourse.bass as bass
from concourse import mybir

ALU = mybir.AluOpType
ACT = mybir.ActivationFunctionType
AX = mybir.AxisListType
F32 = mybir.dt.float32
F32R = mybir.dt.float32r

P = 128
RING = 4
META, SEQ, D = 16, 256, 2048
T = META + SEQ
KT = D // P
FT = 5504 // P
CHUNKS = (16, 16, FT - 32)
UB = 16
LT = 8
HEAD = 64
EPS = 1e-6
GELU_CUBIC = 0.044715
GELU_SIGMOID = 2.0 * 0.7978845608028654
CV0 = META - 2



def ffn_plan(unit, out, hid):
    plan = []
    for nf in CHUNKS:
        plan.append(dict(gu_u=unit, gu_o=out, f0=hid, nf=nf, dn_u=unit + 2 * nf, dn_o=out + 2 * nf))
        unit += 2 * nf + nf * KT // UB
        out += 2 * nf + KT
        hid += nf
    return plan, unit, out, hid


FFN1, IN_U, IN_O, HID1 = ffn_plan(0, 0, 0)
OUT_U, OUT_O = IN_U + 5 * LT, IN_O + 5 * LT
FFN2, UNITS, OUTPUTS, _ = ffn_plan(OUT_U + KT, OUT_O + KT, HID1)
LAST_DOWN = CHUNKS[2]
SPLIT_AT = 6
WARM_START, WARM_SQUARE, WARM_ROOT = 18, 1, 16
RESULT = ((0, 2), (2, 6), (6, 10), (10, 14), (14, 16))
SUM_BLOCK = 14
PIECES = ((0, 2), (2, 4), (4, 8), (8, 12), (12, 16))

VEC = {}
_at = 0
for _name, _n in (("ffn1_pre_g", KT), ("ffn1_post_g", KT), ("mix_pre_g", KT), ("mix_post_g", KT),
                  ("ffn2_pre_g", KT), ("ffn2_post_g", KT), ("lru_conv_w", 4 * LT), ("lru_conv_b", LT),
                  ("lru_b_a", LT), ("lru_b_x", LT), ("lru_lambda", LT), ("sconv_w", 3 * LT),
                  ("lru_out_g", LT), ("sconv_out_g", LT)):
    VEC[_name] = _at
    _at += _n
NVEC = _at
DECAY_POS, DECAY_NEG = NVEC, NVEC + LT
SCRATCH = NVEC + 2 * LT
EPS_COL = SCRATCH + 4 * LT
VCOLS = EPS_COL + 1


def outputs_through(j):
    return -(-UB * (j + 1) // LAST_DOWN)


def hymba_layer_kernel(nc, xt, weights, gates, vectors, out):
    with ExitStack() as ctx:
        at = [16512]

        def sb(name, shape, dt=F32, offset=None):
            size = 4
            for n in shape[1:]:
                size *= n
            if offset is None:
                offset = at[0]
                at[0] += -(-size // 32) * 32
            return nc.alloc_sbuf_tensor_at(name, shape, dt, offset=offset)

        def sem(name):
            return ctx.enter_context(nc.semaphore(name))

        raw = sb("raw", [P, RING, UB * P])
        w_hi = sb("w_hi", [P, RING, UB * P], F32R)
        w_lo = sb("w_lo", [P, RING, UB * P], F32R)
        h = sb("h", [P, KT, T])
        x_hi = sb("x_hi", [P, KT, T], F32R)
        x_lo = sb("x_lo", [P, KT, T], F32R)
        hid_hi = sb("hid_hi", [P, CHUNKS[0], T], F32R)
        hid_lo = sb("hid_lo", [P, CHUNKS[0], T], F32R)
        facc_at = at[0]
        facc = sb("facc", [P, KT, T])
        rms = sb("rms", [P, T])
        ssum = sb("ssum", [P, T])
        sq = sb("sq", [P, T])
        tg = sb("tg", [P, T])
        tu = sb("tu", [P, T])
        ones = sb("ones", [P, P])
        head_ones = sb("head_ones", [P, P])
        vec = sb("vec", [P, VCOLS])
        zx = sb("zx", [P, 3 + T])
        gate_diag = sb("gate_diag", [P, 2, P])
        assert at[0] <= 229344, at[0]

        mat = [facc_at]

        def over(name, shape):
            size = 4
            for n in shape[1:]:
                size *= n
            t = sb(name, shape, F32, offset=mat[0])
            mat[0] += -(-size // 32) * 32
            return t

        gate_w = over("gate_w", [P, 2, LT, HEAD])
        xc = over("xc", [P, T])
        yz = over("yz", [P, SEQ])
        y3 = over("y3", [P, SEQ])
        bz = over("bz", [P, SEQ])
        cz = over("cz", [P, T - CV0])
        cv = over("cv", [P, T - CV0])
        decay = over("decay", [P, T])
        inject = over("inject", [P, T])
        o_both = over("o_both", [P, 2, SEQ])
        head_sq = over("head_sq", [P, 2, SEQ])
        assert mat[0] <= facc_at + 4 * KT * T, mat[0] - facc_at
        o_lru, o_sc = o_both[:, 0, :], o_both[:, 1, :]
        gx, scan, gy = tu, tg, sq

        bank = [nc.alloc_psum_tensor(f"bank{n}", [P, 512], F32) for n in range(8)]
        GATE_A, GATE_X, HEAD_SUM, TOKEN_SUM = bank[4], bank[5], bank[6], bank[7]

        raw_in = [sem(f"raw_in{n}") for n in range(RING)]
        pair_in = [sem(f"pair_in{n}") for n in range(len(PIECES))]
        pair_hi_done = sem("pair_hi_done")
        pair_lo_done = sem("pair_lo_done")
        w_hi_done = sem("w_hi_done")
        w_lo_done = sem("w_lo_done")
        out_done = sem("out_done")
        out_taken = sem("out_taken")
        x_in = [sem(f"x_in{n}") for n in range(len(PIECES))]
        vec_in = sem("vec_in")
        gate_w_in = sem("gate_w_in")
        consts_set = sem("consts_set")
        h_ready = sem("h_ready")
        x_hi_done = sem("x_hi_done")
        x_lo_done = sem("x_lo_done")
        h_sq_done = sem("h_sq_done")
        ssum_ready = sem("ssum_ready")
        token_sum_done = sem("token_sum_done")
        facc_scaled = sem("facc_scaled")
        root_done = sem("root_done")
        raw_scaled = sem("raw_scaled")
        silu_done = sem("silu_done")
        hidden_ready = sem("hidden_ready")
        hid_hi_done = sem("hid_hi_done")
        hid_lo_done = sem("hid_lo_done")
        sq_done = sem("sq_done")
        sq_added = sem("sq_added")
        tap0_done = sem("tap0_done")
        xc_ready = sem("xc_ready")
        y_sq_done = sem("y_sq_done")
        y3_ready = sem("y3_ready")
        gelu_gate_done = sem("gelu_gate_done")
        gate_diag_ready = sem("gate_diag_ready")
        gates_done = sem("gates_done")
        decay_ready = sem("decay_ready")
        inject_sq_ready = sem("inject_sq_ready")
        inject_ready = sem("inject_ready")
        lru_out_ready = sem("lru_out_ready")
        sc_out_ready = sem("sc_out_ready")
        head_sq_done = sem("head_sq_done")
        head_sum_done = sem("head_sum_done")
        head_root_done = sem("head_root_done")
        mixed_ready = sem("mixed_ready")
        mixed_hi_done = sem("mixed_hi_done")
        mixed_lo_done = sem("mixed_lo_done")
        act_order = sem("act_order")
        dve_order = sem("dve_order")
        exp_lambda_done = sem("exp_lambda_done")
        lambda_abs_ready = sem("lambda_abs_ready")
        decay_rate_ready = sem("decay_rate_ready")
        eps_set = sem("eps_set")
        out_gained = sem("out_gained")
        out_scaled = sem("out_scaled")
        out_ready = sem("out_ready")
        stored = sem("stored")

        def col(name, k=0):
            c = (VEC[name] if isinstance(name, str) else name) + k
            return vec[:, bass.ds(c, 1)] if not isinstance(c, int) else vec[:, c:c + 1]

        def psum(o, n):
            return bank[o % RING][:, 0:n]

        def tile_of(buf, k, c0=0, c1=T):
            if isinstance(k, int):
                return buf[:, k, c0:c1]
            return buf[:, bass.ds(k, 1), c0:c1].rearrange("p a t -> p (a t)")

        block = ctx.enter_context(nc.Block())

        @block.sync
        def _(sp):
            def load_unit(v, slot):
                sp.dma_start(raw[:, slot], weights[v]).then_inc(raw_in[slot], 16)

            for n, (k0, k1) in enumerate(PIECES):
                sp.dma_start(h[:, k0:k1, :], xt[:, k0:k1, :]).then_inc(x_in[n], 16)
                part = slice(k0 * P, k1 * P)
                for v in range(2):
                    sp.dma_start(raw[:, v, part], weights[v][:, part]).then_inc(pair_in[n], 16)
            for v in range(2, RING):
                load_unit(v, v)
            loops = (UNITS - RING) // RING
            with sp.Fori(0, loops) as i:
                for j in range(RING):
                    sp.wait_ge(w_lo_done, i * RING + (j + 1))
                    src = weights[bass.ds(i * RING + (RING + j), 1)].rearrange("a p n -> (a p) n")
                    sp.dma_start(raw[:, j], src).then_inc(raw_in[j], 16)
            for v in range(RING + loops * RING, UNITS):
                sp.wait_ge(w_lo_done, v - RING + 1)
                load_unit(v, v % RING)
            for g, (k0, k1) in enumerate(RESULT):
                sp.wait_ge(out_ready, g + 1)
                sp.dma_start(out[:, k0:k1, :], facc[:, k0:k1, META:T]).then_inc(stored, 16)
            sp.wait_ge(stored, len(RESULT) * 16)

        @block.gpsimd
        def _(pool):
            pool.memset(ones[:], 1.0)
            pool.memset(zx[:, 0:3], 0.0)
            pool.memset(gate_diag[:], 0.0)
            pool.memset(head_ones[:], 0.0).then_inc(consts_set, 1)
            pool.wait_ge(consts_set, 1)
            pool.memset(head_ones[0:HEAD, 0:HEAD], 1.0)
            pool.memset(head_ones[HEAD:P, HEAD:P], 1.0).then_inc(consts_set, 1)
            pool.wait_ge(ssum_ready, 2)
            pool.dma_start(gate_w[:], gates).then_inc(gate_w_in, 16)
            pool.wait_ge(gate_w_in, 16)
            for t in range(LT):
                if t:
                    pool.wait_ge(gates_done, t)
                pool.tensor_copy(gate_diag[0:HEAD, :, 0:HEAD], gate_w[0:HEAD, :, t, :])
                pool.tensor_copy(gate_diag[HEAD:P, :, HEAD:P], gate_w[HEAD:P, :, t, :]).then_inc(gate_diag_ready, 1)

        @block.tensor
        def _(pe):
            def three(o, slot, b, mov_hi, mov_lo, first, last):
                hi, lo = w_hi[:, slot, b * P:(b + 1) * P], w_lo[:, slot, b * P:(b + 1) * P]
                acc = psum(o, mov_hi.shape[-1])
                pe.matmul(acc, hi, mov_hi, start=first, stop=False)
                pe.matmul(acc, hi, mov_lo, start=False, stop=False)
                mm = pe.matmul(acc, lo, mov_hi, start=False, stop=last)
                if last:
                    mm.then_inc(out_done, 1)

            def unit_ready(u, i=0):
                pe.wait_ge(w_lo_done, i * RING + (u + 1))

            def bank_free(o, i=0):
                if not isinstance(i, int) or o >= RING:
                    pe.wait_ge(out_taken, i * RING + (o - RING + 1))

            def unit(u, o, hi, lo, c0, c1, i=0, ready=(), between=None):
                unit_ready(u, i)
                bank_free(o, i)
                for k in range(UB):
                    if k in ready:
                        pe.wait_ge(*ready[k])
                    if between and k == between[0]:
                        between[1]()
                    three(o, u % RING, k, hi[:, k, c0:c1], lo[:, k, c0:c1], k == 0, k == UB - 1)

            def first_four(u, o, hi, lo, cols, ready, order=range(UB), together=13, after=None):
                order, lag = list(order), SPLIT_AT + 1
                steps = []
                for n in range(together):
                    steps += [(s, n) for s in range(3)]
                    if n >= lag:
                        steps.append((3, n - lag))
                steps += [(s, n) for s in range(3) for n in range(together, UB)]
                steps += [(3, n) for n in range(together - lag, UB)]
                for at, (s, n) in enumerate(steps):
                    k, (c0, c1) = order[n], cols[s]
                    if n == 0:
                        unit_ready(u + s)
                        bank_free(o + s)
                    if s == 0 and k in ready:
                        pe.wait_ge(*ready[k])
                    three(o + s, (u + s) % RING, k, hi[:, k, c0:c1], lo[:, k, c0:c1], n == 0, n == UB - 1)
                    if after and at == after[0]:
                        after[1]()

            def output_token_sum(c0, squares):
                keep_warm(WARM_SQUARE)
                pe.wait_ge(sq_added, squares)
                pe.matmul(TOKEN_SUM[:, c0:T], ones[:], ssum[:, c0:T], start=True, stop=False)
                keep_warm(WARM_SQUARE)
                pe.wait_ge(sq_done, squares)
                pe.matmul(TOKEN_SUM[:, c0:T], ones[:], sq[:, c0:T], start=False, stop=True).then_inc(token_sum_done, 1)

            def token_sum(count, c0):
                pe.wait_ge(ssum_ready, count)
                pe.matmul(TOKEN_SUM[:, c0:T], ones[:], ssum[:, c0:T], start=True, stop=True).then_inc(token_sum_done, 1)

            def keep_warm(n):
                for _ in range(n):
                    pe.matmul(HEAD_SUM[:, 0:P], ones[:], head_ones[:], start=True, stop=True)

            def operand_tiles(first):
                return {k: (x_lo_done, first + k + 1) for k in range(KT)}

            def ffn(plan, c0, operand, sums, squares):
                n = T - c0
                for c, q in enumerate(plan):
                    u, o, units = q["gu_u"], q["gu_o"], 2 * q["nf"]
                    if c == 0:
                        if u == 0:
                            for g, (k0, k1) in enumerate(PIECES):
                                if k1 < UB:
                                    pe.wait_ge(pair_lo_done, 2 * (g + 1))
                                else:
                                    unit_ready(1)
                                for k in range(k0, k1):
                                    pe.wait_ge(x_lo_done, k + 1)
                                    for v in range(2):
                                        three(v, v, k, x_hi[:, k], x_lo[:, k], k == 0, k == UB - 1)
                            unit(2, 2, x_hi, x_lo, c0, T)
                            unit(3, 3, x_hi, x_lo, c0, T)
                        else:
                            first_four(u, o, x_hi, x_lo, [(c0, T)] * RING, operand_tiles(operand))
                        u, o, units = u + RING, o + RING, units - 2 * RING
                        for j in range(RING):
                            unit(u + j, o + j, x_hi, x_lo, c0, T,
                                 between=(SUM_BLOCK, lambda: token_sum(sums, c0)) if j == 0 else None)
                        u, o = u + RING, o + RING
                    with pe.Fori(0, units // RING) as i:
                        for j in range(RING):
                            unit(u + j, o + j, x_hi, x_lo, c0, T, i)
                    for j in range(units - units % RING, units):
                        unit(u + j, o + j, x_hi, x_lo, c0, T)
                    u, o, nf = q["dn_u"], q["dn_o"], q["nf"]
                    late = {k: (hid_lo_done, q["f0"] + k + 1) for k in (nf - 3, nf - 2, nf - 1)}
                    if nf == UB:
                        with pe.Fori(0, KT // RING) as i:
                            for j in range(RING):
                                unit(u + j, o + j, hid_hi, hid_lo, 0, n, i, late if j == 0 else ())
                    else:
                        for m in range(KT):
                            bank_free(o + m)
                            for k in range(nf):
                                b = m * nf + k
                                if b % UB == 0:
                                    unit_ready(u + b // UB)
                                if m == 0 and k in late:
                                    pe.wait_ge(*late[k])
                                three(o + m, (u + b // UB) % RING, b % UB, hid_hi[:, k, 0:n], hid_lo[:, k, 0:n],
                                      k == 0, k == nf - 1)
                output_token_sum(c0, squares + KT)
                if plan is FFN1:
                    keep_warm(WARM_ROOT)

            def head_products(t):
                pe.wait_ge(xc_ready, t + 1)
                pe.wait_ge(gate_diag_ready, t + 1)
                pe.matmul(GATE_A[:, 0:T], gate_diag[:, 0, :], xc[:], start=True, stop=True)
                pe.matmul(GATE_X[:, 0:T], gate_diag[:, 1, :], xc[:], start=True, stop=True).then_inc(gates_done, 1)

            def head_sums(t):
                pe.wait_ge(head_sq_done, t + 1)
                pe.matmul(HEAD_SUM[:, :], head_ones[:], head_sq[:].rearrange("p a t -> p (a t)"),
                          start=True, stop=True).then_inc(head_sum_done, 1)

            pe.wait_ge(consts_set, 2)
            keep_warm(WARM_START)
            ffn(FFN1, 0, 0, 1, 0)

            cols = [(0, T), (META, T), (META, T), (CV0, T), (CV0, T)]
            first_four(IN_U, IN_O, x_hi, x_lo, cols, operand_tiles(KT))
            unit(IN_U + 4, IN_O + 4, x_hi, x_lo, *cols[4], between=(SUM_BLOCK, lambda: token_sum(2, 0)))
            for t in range(1, LT):
                u, o = IN_U + 5 * t, IN_O + 5 * t
                for z in range(5):
                    between = (1, lambda: head_products(0)) if t == 1 and z == 1 else None
                    unit(u + z, o + z, x_hi, x_lo, *cols[z], between=between)
                    if z == (3 if t < 4 else 2):
                        head_products(t)
                        head_sums(t - 1)

            order = [*range(LT - 2), *range(LT, 2 * LT - 2), LT - 2, 2 * LT - 2, LT - 1, 2 * LT - 1]
            first_four(OUT_U, OUT_O, hid_hi, hid_lo, [(META, T)] * RING,
                       {0: (mixed_lo_done, LT - 2), LT - 2: (mixed_lo_done, LT - 1), LT - 1: (mixed_lo_done, LT)},
                       order, together=14, after=(29, lambda: head_sums(LT - 1)))
            with pe.Fori(0, KT // RING - 1) as i:
                for j in range(RING):
                    unit(OUT_U + RING + j, OUT_O + RING + j, hid_hi, hid_lo, META, T, i)
            output_token_sum(META, 2 * KT)
            keep_warm(WARM_ROOT)

            ffn(FFN2, META, 2 * KT, 3, 2 * KT)

        @block.scalar
        def _(act):
            links = [0]

            def link(instruction):
                links[0] += 1
                instruction.then_inc(act_order, 1)
                act.wait_ge(act_order, links[0])

            def split_head(v, used, i=0):
                slot = v % RING
                act.wait_ge(raw_in[slot], i * 16 + 16 * (v // RING + (1 if slot > 1 else 0)))
                if used:
                    act.wait_ge(out_done, i * RING + used)
                act.activation(w_hi[:, slot], raw[:, slot], ACT.Copy).then_inc(w_hi_done, 1)

            def root(count, c0):
                act.wait_ge(token_sum_done, count)
                act.activation(rms[:, c0:T], TOKEN_SUM[:, c0:T], ACT.Sqrt, bias=col(EPS_COL),
                               scale=1.0 / D).then_inc(root_done, 1)

            def operand_head(k, gain, c0):
                act.activation(x_hi[:, k, c0:T], h[:, k, c0:T], ACT.Copy, scale=col(gain, k)).then_inc(x_hi_done, 1)

            def square_h(k, c0):
                act.activation(facc[:, k, c0:T], h[:, k, c0:T], ACT.Square).then_inc(h_sq_done, 1)

            def operand_heads(gain, c0, renewed):
                for k in range(KT):
                    act.wait_ge(h_ready, renewed + k + 1)
                    operand_head(k, gain, c0)
                    square_h(k, c0)

            def gate_up(u, o, f, k, n, i=0, last=False):
                split_head(u + RING, o + 1, i)
                act.wait_ge(out_taken, i * RING + (o + 1))
                act.activation(sq[:, 0:n], tg[:, 0:n], ACT.Silu).then_inc(silu_done, 1)
                if last:
                    act.wait_ge(hidden_ready, f + 1)
                    hidden_head(k, n)
                split_head(u + 1 + RING, o + 2, i)
                if not last:
                    act.wait_ge(hidden_ready, i * 2 + (f + 1))
                    hidden_head(k, n)

            def first_two(u, o, f, n, c0, sums, scaled):
                if u == 0:
                    for k in range(KT // 2):
                        square_h(k, c0)
                split_head(u + RING, o + 1)
                if u == 0:
                    for k in range(KT // 2, KT):
                        square_h(k, c0)
                split_head(u + 1 + RING, o + 2)
                root(sums, c0)
                split_head(u + 2 + RING, o + 3)
                split_head(u + 3 + RING, o + 4)
                for k in range(2):
                    act.wait_ge(raw_scaled, scaled + k + 1)
                    act.activation(sq[:, 0:n], tg[:, 0:n], ACT.Silu).then_inc(silu_done, 1)
                    act.wait_ge(hidden_ready, f + k + 1)
                    hidden_head(k, n)

            def hidden_head(k, n):
                act.activation(tile_of(hid_hi, k, 0, n), tu[:, 0:n], ACT.Copy).then_inc(hid_hi_done, 1)

            def square_output(k, c0, o, first, i=0):
                act.wait_ge(out_taken, i * RING + (o + 1))
                act.wait_ge(sq_added, i * RING + (first + 1))
                act.activation(sq[:, c0:T], tile_of(facc, k, c0), ACT.Square).then_inc(sq_done, 1)

            def gain_output(gain, k, c0, first):
                act.wait_ge(sq_done, first + 1)
                act.activation(facc[:, k, c0:T], facc[:, k, c0:T], ACT.Copy, scale=col(gain, k)).then_inc(out_gained, 1)

            def ffn(plan, c0, squares, sums, scaled, gain=None):
                n = T - c0
                for c, q in enumerate(plan):
                    u, o, f0, nf = q["gu_u"], q["gu_o"], q["f0"], q["nf"]
                    first = 0
                    if c == 0:
                        first_two(u, o, f0, n, c0, sums, scaled)
                        first = 2
                    act.preload_act_table(ACT.Silu)
                    with act.Fori(0, (nf - first) // 2) as i:
                        for j in range(first, first + 2):
                            gate_up(u + 2 * j, o + 2 * j, f0 + j, i * 2 + j, n, i)
                    if nf % 2:
                        gate_up(u + 2 * nf - 2, o + 2 * nf - 2, f0 + nf - 1, nf - 1, n, last=True)
                    u, o = q["dn_u"], q["dn_o"]
                    if nf == UB:
                        with act.Fori(0, KT // RING) as i:
                            for j in range(RING):
                                split_head(u + j + RING, o + j + 1, i)
                        if plan is FFN1 and c == 0:
                            act.wait_ge(lambda_abs_ready, 1)
                            act.activation(vec[:, SCRATCH:SCRATCH + LT], vec[:, SCRATCH:SCRATCH + LT], ACT.Exp,
                                           scale=-1.0).then_inc(exp_lambda_done, 1)
                        continue
                    act.preload_act_table(ACT.Sqrt)
                    m = 0
                    for j in range(nf):
                        done = outputs_through(j)
                        while m < done:
                            if m == done - 1 and u + j + RING < UNITS and j < nf - 1:
                                split_head(u + j + RING, o + done)
                            square_output(m, c0, o + m, squares + m)
                            if gain and m < KT - 1:
                                gain_output(gain, m, c0, squares + m)
                            m += 1
                    root(sums + 1, c0)
                    if gain:
                        gain_output(gain, KT - 1, c0, squares + KT - 1)
                    if u + nf - 1 + RING < UNITS:
                        split_head(u + nf - 1 + RING, o + KT)

            act.dma_start(vec[:, 0:NVEC], vectors).then_inc(vec_in, 16)
            act.preload_act_table(ACT.Sqrt)
            act.wait_ge(vec_in, 16)
            for g, (k0, k1) in enumerate(PIECES):
                act.wait_ge(x_in[g], 16)
                for k in range(k0, k1):
                    operand_head(k, "ffn1_pre_g", 0)
                act.wait_ge(pair_in[g], 32)
                part = slice(k0 * P, k1 * P)
                for v in range(2):
                    act.activation(w_hi[:, v, part], raw[:, v, part], ACT.Copy).then_inc(
                        pair_hi_done if k1 < UB else w_hi_done, 1)
            split_head(2, 0)
            split_head(3, 0)
            act.wait_ge(eps_set, 1)
            ffn(FFN1, 0, 0, 1, 0)
            operand_heads("mix_pre_g", 0, 0)

            def square_lru(t):
                act.wait_ge(lru_out_ready, t + 1)
                act.activation(head_sq[:, 0, :], o_lru, ACT.Square).then_inc(head_sq_done, 1)

            def head_root(t):
                act.wait_ge(head_sum_done, t + 1)
                act.activation(head_sq[:].rearrange("p a t -> p (a t)"), HEAD_SUM[:, :], ACT.Sqrt, bias=col(EPS_COL),
                               scale=1.0 / HEAD).then_inc(head_root_done, 1)

            def mixed_heads(t):
                act.wait_ge(mixed_ready, t + 1)
                act.activation(hid_hi[:, t, META:T], o_lru, ACT.Copy, scale=col("lru_out_g", t))
                act.activation(hid_hi[:, LT + t, META:T], o_sc, ACT.Copy,
                               scale=col("sconv_out_g", t)).then_inc(mixed_hi_done, 1)

            split_head(IN_U + RING, IN_O + 1)
            split_head(IN_U + 1 + RING, IN_O + 2)
            root(3, 0)
            split_head(IN_U + 2 + RING, IN_O + 3)
            def gates(t):
                act.wait_ge(gates_done, t + 1)
                act.activation(gx[:], GATE_X[:, 0:T], ACT.Sigmoid, bias=col("lru_b_x", t))
                link(act.activation(decay[:], GATE_A[:, 0:T], ACT.Sigmoid, bias=col("lru_b_a", t)))
                link(act.activation(inject[:], decay[:], ACT.Tanh, scale=col(DECAY_POS, t)))
                link(act.activation(decay[:], decay[:], ACT.Exp, scale=col(DECAY_NEG, t)))
                act.activation(scan[:], decay[:], ACT.Square).then_inc(decay_ready, 1)
                if t == LT - 1:
                    split_head(IN_U + 5 * t + 3 + RING, IN_O + 5 * t + 4)
                if t:
                    head_root(t - 1)
                act.wait_ge(inject_sq_ready, t + 1)
                act.activation(inject[:], inject[:], ACT.Sqrt).then_inc(inject_ready, 1)

            def tap0(t):
                act.activation(xc[:], zx[:, 0:T], ACT.Identity, bias=col("lru_conv_b", t),
                               scale=col("lru_conv_w", t)).then_inc(tap0_done, 1)

            def square_y():
                act.activation(y3[:], yz[:], ACT.Square, scale=GELU_CUBIC ** 0.5).then_inc(y_sq_done, 1)

            def gelu_gate(t):
                act.wait_ge(y3_ready, t + 1)
                act.activation(gy[:, 0:SEQ], y3[:], ACT.Sigmoid, scale=GELU_SIGMOID).then_inc(gelu_gate_done, 1)

            def square_sc(t):
                act.wait_ge(sc_out_ready, t + 1)
                act.activation(head_sq[:, 1, :], o_sc, ACT.Square)

            act.wait_ge(raw_scaled, 3)
            tap0(0)
            act.wait_ge(raw_scaled, 4)
            square_y()
            split_head(IN_U + 3 + RING, IN_O + 4)
            split_head(IN_U + 4 + RING, IN_O + 5)
            gelu_gate(0)
            act.wait_ge(decay_rate_ready, 1)
            gates(0)
            square_sc(0)
            for t in range(1, LT):
                u, o = IN_U + 5 * t, IN_O + 5 * t
                split_head(u + RING, o + 1)
                act.wait_ge(out_taken, o + 1)
                tap0(t)
                square_lru(t - 1)
                split_head(u + 1 + RING, o + 2)
                act.wait_ge(out_taken, o + 2)
                square_y()
                split_head(u + 2 + RING, o + 3)
                gelu_gate(t)
                gates(t)
                if t < LT - 1:
                    split_head(u + 3 + RING, o + 4)
                split_head(u + 4 + RING, o + 5)
                mixed_heads(t - 1)
                square_sc(t)
            square_lru(LT - 1)
            head_root(LT - 1)
            mixed_heads(LT - 1)

            act.preload_act_table(ACT.Sqrt)
            with act.Fori(0, KT // RING - 1) as i:
                for j in range(RING):
                    split_head(OUT_U + j + RING, OUT_O + j + 1, i)
                    square_output(i * RING + j, META, OUT_O + j, KT + j, i)
            for j in range(KT - RING, KT - 1):
                split_head(OUT_U + j + RING, OUT_O + j + 1)
                square_output(j, META, OUT_O + j, KT + j)
            square_output(KT - 1, META, OUT_O + KT - 1, 2 * KT - 1)
            root(4, META)
            split_head(OUT_U + KT - 1 + RING, OUT_O + KT)
            operand_heads("ffn2_pre_g", META, KT)
            ffn(FFN2, META, 2 * KT, 5, 4, "ffn2_post_g")

        @block.vector
        def _(dve):
            links = [0]

            def link(instruction):
                links[0] += 1
                instruction.then_inc(dve_order, 1)
                dve.wait_ge(dve_order, links[0])

            def split_rest(v, i=0):
                slot = v % RING
                dve.wait_ge(w_hi_done, i * RING + (v + 1))
                dve.tensor_tensor(w_lo[:, slot], raw[:, slot], w_hi[:, slot].bitcast(F32),
                                  ALU.subtract).then_inc(w_lo_done, 1)

            def operand_rest(k, gain, c0, first):
                dve.wait_ge(x_hi_done, first + k + 1)
                dve.scalar_tensor_tensor(x_lo[:, k, c0:T], h[:, k, c0:T], col(gain, k), x_hi[:, k, c0:T].bitcast(F32),
                                         ALU.mult, ALU.subtract).then_inc(x_lo_done, 1)

            def sum_h_squares(half, c0, first):
                k = half * KT // 2
                into = sq if half else ssum
                dve.wait_ge(h_sq_done, first + k + KT // 2)
                link(dve.tensor_reduce(into[:, c0:T], facc[:, k:k + KT // 2, c0:T].rearrange("p k t -> p t k"), AX.X,
                                       ALU.add))
                if half:
                    dve.tensor_tensor(ssum[:, c0:T], ssum[:, c0:T], sq[:, c0:T], ALU.add).then_inc(ssum_ready, 1)

            def token_rms(count, c0):
                dve.wait_ge(root_done, count)
                link(dve.reciprocal(rms[:, c0:T], rms[:, c0:T]))

            def new_residual(post, pre, c0, lo_first, v):
                for k in range(KT + 1):
                    if k < KT:
                        dve.tensor_tensor(facc[:, k, c0:T], facc[:, k, c0:T], rms[:, c0:T], ALU.mult).then_inc(
                            facc_scaled, 1)
                    if k:
                        dve.wait_ge(facc_scaled, lo_first - KT + k)
                        dve.scalar_tensor_tensor(h[:, k - 1, c0:T], facc[:, k - 1, c0:T], col(post, k - 1),
                                                 h[:, k - 1, c0:T], ALU.mult, ALU.add).then_inc(h_ready, 1)
                    if k > 1:
                        operand_rest(k - 2, pre, c0, lo_first)
                    if k == SPLIT_AT:
                        split_rest(v)
                operand_rest(KT - 1, pre, c0, lo_first)

            def take_raw(o, buf):
                dve.wait_ge(out_done, o + 1)
                dve.tensor_copy(buf, psum(o, buf.shape[-1])).then_inc(out_taken, 1)

            def add_square(count, c0, i=0):
                dve.wait_ge(sq_done, i * RING + (count + 1))
                dve.tensor_tensor(ssum[:, c0:T], ssum[:, c0:T], sq[:, c0:T], ALU.add).then_inc(sq_added, 1)

            def clear_sum(c0):
                dve.memset(ssum[:, c0:T], 0.0).then_inc(sq_added, 1)

            def hidden_rest(f, k, n, i=0):
                dve.wait_ge(hid_hi_done, i * 2 + (f + 1))
                dve.tensor_tensor(tile_of(hid_lo, k, 0, n), tu[:, 0:n], tile_of(hid_hi, k, 0, n).bitcast(F32),
                                  ALU.subtract).then_inc(hid_lo_done, 1)

            def gate_up(u, o, f, k, n, i=0, last=False):
                c0 = T - n
                dve.wait_ge(out_done, i * RING + (o + 1))
                dve.tensor_tensor(tg[:, 0:n], psum(o, n), rms[:, c0:T], ALU.mult).then_inc(out_taken, 1)
                split_rest(u + RING, i)
                dve.wait_ge(out_done, i * RING + (o + 2))
                dve.wait_ge(w_lo_done, i * RING + (u + RING + 1))
                dve.tensor_tensor(tu[:, 0:n], psum(o + 1, n), rms[:, c0:T], ALU.mult).then_inc(out_taken, 1)
                dve.wait_ge(out_taken, i * RING + (o + 2))
                dve.wait_ge(silu_done, i * 2 + (f + 1))
                dve.tensor_tensor(tu[:, 0:n], tu[:, 0:n], sq[:, 0:n], ALU.mult).then_inc(hidden_ready, 1)
                if last:
                    hidden_rest(f, k, n)
                split_rest(u + 1 + RING, i)
                if not last:
                    hidden_rest(f, k, n, i)

            def first_two(u, o, f, n, sums, h_squares):
                c0 = T - n
                gates, ups = (tg[:, 0:n], facc[:, 0, 0:n]), (tu[:, 0:n], facc[:, 1, 0:n])
                take_raw(o, gates[0])
                split_rest(u + RING)
                sum_h_squares(0, c0, h_squares)
                take_raw(o + 1, ups[0])
                sum_h_squares(1, c0, h_squares)
                split_rest(u + 1 + RING)
                token_rms(sums, c0)
                take_raw(o + 2, gates[1])
                split_rest(u + 2 + RING)
                take_raw(o + 3, ups[1])
                dve.wait_ge(out_taken, o + 4)
                for k in range(2):
                    dve.tensor_tensor(tg[:, 0:n], gates[k], rms[:, c0:T], ALU.mult).then_inc(raw_scaled, 1)
                    if k:
                        dve.wait_ge(hid_lo_done, f + k)
                    link(dve.tensor_tensor(tu[:, 0:n], ups[k], rms[:, c0:T], ALU.mult))
                    dve.wait_ge(silu_done, f + k + 1)
                    dve.tensor_tensor(tu[:, 0:n], tu[:, 0:n], sq[:, 0:n], ALU.mult).then_inc(hidden_ready, 1)
                    if k == 0:
                        split_rest(u + 3 + RING)
                    hidden_rest(f + k, k, n)

            def ffn(plan, c0, squares, sums):
                n = T - c0
                for c, q in enumerate(plan):
                    u, o, f0, nf = q["gu_u"], q["gu_o"], q["f0"], q["nf"]
                    first = 0
                    if c == 0:
                        first_two(u, o, f0, n, sums, squares)
                        first = 2
                    with dve.Fori(0, (nf - first) // 2) as i:
                        for j in range(first, first + 2):
                            gate_up(u + 2 * j, o + 2 * j, f0 + j, i * 2 + j, n, i)
                    if nf % 2:
                        gate_up(u + 2 * nf - 2, o + 2 * nf - 2, f0 + nf - 1, nf - 1, n, last=True)
                    if plan is FFN1 and c == 0:
                        small_vectors()
                    u, o = q["dn_u"], q["dn_o"]

                    def down(m, at, i=0):
                        dve.wait_ge(out_done, i * RING + (at + 1))
                        f = tile_of(facc, m, c0)
                        if c == 0:
                            dve.tensor_copy(f, psum(at, n)).then_inc(out_taken, 1)
                        else:
                            dve.tensor_tensor(f, psum(at, n), f, ALU.add).then_inc(out_taken, 1)

                    if nf == UB:
                        with dve.Fori(0, KT // RING) as i:
                            for j in range(RING):
                                down(i * RING + j, o + j, i)
                                split_rest(u + j + RING, i)
                        if plan is FFN1 and c == 0:
                            decay_rates()
                        continue
                    m = 0
                    for j in range(nf):
                        done = outputs_through(j)
                        while m < done:
                            down(m, o + m)
                            if m == 0:
                                clear_sum(c0)
                            if m == done - 1 and u + j + RING < UNITS and j < nf - 1:
                                split_rest(u + j + RING)
                            if m < KT - 1:
                                add_square(squares + m, c0)
                            m += 1

            lam = vec[:, VEC["lru_lambda"]:VEC["lru_lambda"] + LT]
            e, s, s2, poly = (vec[:, SCRATCH + n * LT:SCRATCH + (n + 1) * LT] for n in range(4))
            rate, minus = vec[:, DECAY_POS:DECAY_POS + LT], vec[:, DECAY_NEG:DECAY_NEG + LT]

            def small_vectors():
                for name in ("ffn1_post_g", "ffn2_post_g"):
                    g = vec[:, VEC[name]:VEC[name] + KT]
                    link(dve.tensor_scalar(g, g, 0.5, None, ALU.mult))
                link(dve.tensor_scalar(minus, lam, -1.0, 0.0, ALU.mult, ALU.max))
                link(dve.tensor_scalar(rate, lam, 0.0, None, ALU.max))
                dve.tensor_tensor(e, rate, minus, ALU.add).then_inc(lambda_abs_ready, 1)

            def decay_rates():
                dve.wait_ge(exp_lambda_done, 1)
                link(dve.tensor_scalar(s2, e, 2.0, None, ALU.add))
                link(dve.reciprocal(s, s2))
                link(dve.tensor_tensor(s, s, e, ALU.mult))
                link(dve.tensor_tensor(s2, s, s, ALU.mult))
                link(dve.tensor_scalar(poly, s2, 2.0 / 17, 2.0 / 15, ALU.mult, ALU.add))
                for n in (13, 11, 9, 7, 5, 3, 1):
                    link(dve.tensor_tensor(poly, poly, s2, ALU.mult))
                    link(dve.tensor_scalar(poly, poly, 2.0 / n, None, ALU.add))
                link(dve.tensor_tensor(poly, poly, s, ALU.mult))
                link(dve.tensor_tensor(poly, poly, minus, ALU.add))
                link(dve.tensor_scalar(rate, poly, 8.0, None, ALU.mult))
                dve.tensor_scalar(minus, poly, -8.0, None, ALU.mult).then_inc(decay_rate_ready, 1)

            dve.memset(col(EPS_COL), EPS).then_inc(eps_set, 1)
            for g, (k0, k1) in enumerate(PIECES):
                for k in range(k0, k1):
                    operand_rest(k, "ffn1_pre_g", 0, 0)
                part = slice(k0 * P, k1 * P)
                for v in range(2):
                    if k1 < UB:
                        dve.wait_ge(pair_hi_done, 2 * g + v + 1)
                    else:
                        dve.wait_ge(w_hi_done, v + 1)
                    dve.tensor_tensor(w_lo[:, v, part], raw[:, v, part], w_hi[:, v, part].bitcast(F32),
                                      ALU.subtract).then_inc(pair_lo_done if k1 < UB else w_lo_done, 1)
            split_rest(2)
            split_rest(3)
            ffn(FFN1, 0, 0, 1)
            token_rms(2, 0)
            new_residual("ffn1_post_g", "mix_pre_g", 0, KT, IN_U + 3)
            def take(o, buf, c0, by):
                dve.wait_ge(out_done, o + 1)
                dve.tensor_tensor(buf, psum(o, T - c0), by[:, c0:T], ALU.mult).then_inc(out_taken, 1)

            def taps(t):
                dve.wait_ge(tap0_done, t + 1)
                for w in range(1, 4):
                    tap = dve.scalar_tensor_tensor(xc[:], zx[:, w:w + T], col("lru_conv_w", w * LT + t), xc[:],
                                                   ALU.mult, ALU.add)
                    if w < 3:
                        link(tap)
                tap.then_inc(xc_ready, 1)

            def recurrence(t):
                dve.wait_ge(inject_ready, t + 1)
                link(dve.tensor_tensor(gx[:], gx[:], inject[:], ALU.mult))
                link(dve.tensor_tensor_scan(scan[:], decay[:], gx[:], 0.0, ALU.mult, ALU.add))
                dve.tensor_tensor(o_lru, scan[:, META:T], gy[:, 0:SEQ], ALU.mult).then_inc(lru_out_ready, 1)

            def normed(t):
                dve.wait_ge(head_root_done, t + 1)
                link(dve.reciprocal(head_sq[:], head_sq[:]))
                dve.tensor_tensor(o_both[:], o_both[:], head_sq[:], ALU.mult).then_inc(mixed_ready, 1)

            def mixed_rests(t):
                dve.wait_ge(mixed_hi_done, t + 1)
                dve.scalar_tensor_tensor(hid_lo[:, t, META:T], o_lru, col("lru_out_g", t),
                                         hid_hi[:, t, META:T].bitcast(F32), ALU.mult, ALU.subtract)
                dve.scalar_tensor_tensor(hid_lo[:, LT + t, META:T], o_sc, col("sconv_out_g", t),
                                         hid_hi[:, LT + t, META:T].bitcast(F32), ALU.mult,
                                         ALU.subtract).then_inc(mixed_lo_done, 1)

            def gelu_argument(t):
                dve.wait_ge(y_sq_done, t + 1)
                dve.scalar_tensor_tensor(y3[:], y3[:], 1.0, yz[:], ALU.add, ALU.mult).then_inc(y3_ready, 1)

            def gated(t):
                dve.wait_ge(gelu_gate_done, t + 1)
                dve.tensor_tensor(gy[:, 0:SEQ], gy[:, 0:SEQ], yz[:], ALU.mult)
                dve.wait_ge(decay_ready, t + 1)
                dve.tensor_tensor(gx[:], gx[:], xc[:], ALU.mult)
                dve.scalar_tensor_tensor(inject[:], scan[:], 1.0, inject[:], ALU.add,
                                         ALU.mult).then_inc(inject_sq_ready, 1)

            def take_v(t):
                o = IN_O + 5 * t
                dve.wait_ge(out_done, o + 5)
                dve.wait_ge(out_taken, o + 4)
                dve.tensor_tensor(cv[:], psum(o + 4, T - CV0), cz[:], ALU.mult).then_inc(out_taken, 1)

            def short_convolution(t):
                dve.wait_ge(out_taken, IN_O + 5 * t + 5)
                if t:
                    dve.wait_ge(mixed_lo_done, t)
                link(dve.tensor_scalar(o_sc, cv[:, 0:SEQ], col("sconv_w", t), None, ALU.mult))
                for w in (1, 2):
                    link(dve.scalar_tensor_tensor(o_sc, cv[:, w:w + SEQ], col("sconv_w", w * LT + t), o_sc,
                                                  ALU.mult, ALU.add))
                dve.tensor_tensor(o_sc, o_sc, bz[:], ALU.mult).then_inc(sc_out_ready, 1)

            rms_sq = ssum
            take_raw(IN_O, zx[:, 3:3 + T])
            split_rest(IN_U + RING)
            sum_h_squares(0, 0, KT)
            take_raw(IN_O + 1, yz[:])
            sum_h_squares(1, 0, KT)
            split_rest(IN_U + 1 + RING)
            token_rms(3, 0)
            take_raw(IN_O + 2, bz[:])
            dve.wait_ge(out_taken, IN_O + 2)
            dve.tensor_tensor(zx[:, 3:3 + T], zx[:, 3:3 + T], rms[:], ALU.mult).then_inc(raw_scaled, 1)
            dve.tensor_tensor(yz[:], yz[:], rms[:, META:T], ALU.mult).then_inc(raw_scaled, 1)
            link(dve.tensor_tensor(rms_sq[:], rms[:], rms[:], ALU.mult))
            taps(0)
            gelu_argument(0)
            split_rest(IN_U + 2 + RING)
            take_raw(IN_O + 3, cz[:])
            dve.wait_ge(out_taken, IN_O + 4)
            dve.tensor_tensor(bz[:], bz[:], rms[:, META:T], ALU.mult)
            link(dve.tensor_tensor(cz[:], cz[:], rms_sq[:, CV0:T], ALU.mult))
            take_v(0)
            split_rest(IN_U + 3 + RING)
            gated(0)
            split_rest(IN_U + 4 + RING)
            short_convolution(0)

            for t in range(1, LT):
                u, o = IN_U + 5 * t, IN_O + 5 * t
                take(o, zx[:, 3:3 + T], 0, rms)
                recurrence(t - 1)
                split_rest(u + RING)
                take(o + 1, yz[:], META, rms)
                taps(t)
                split_rest(u + 1 + RING)
                take(o + 2, bz[:], META, rms)
                gelu_argument(t)
                split_rest(u + 2 + RING)
                gated(t)
                take(o + 3, cz[:], CV0, rms_sq)
                if t == LT - 1:
                    split_rest(u + 3 + RING)
                normed(t - 1)
                if t < LT - 1:
                    split_rest(u + 3 + RING)
                take_v(t)
                split_rest(u + 4 + RING)
                mixed_rests(t - 1)
                short_convolution(t)
            recurrence(LT - 1)
            normed(LT - 1)
            mixed_rests(LT - 1)

            def out_tile(m, j, i=0):
                at = OUT_O + j
                dve.wait_ge(out_done, i * RING + (at + 1))
                dve.tensor_copy(tile_of(facc, m, META), psum(at, SEQ)).then_inc(out_taken, 1)

            dve.wait_ge(out_taken, OUT_O)
            clear_sum(META)
            with dve.Fori(0, KT // RING - 1) as i:
                for j in range(RING):
                    out_tile(i * RING + j, j, i)
                    split_rest(OUT_U + j + RING, i)
                    add_square(KT + j, META, i=i)
            for j in range(KT - RING, KT - 1):
                out_tile(j, j)
                split_rest(OUT_U + j + RING)
                add_square(KT + j, META)
            out_tile(KT - 1, KT - 1)
            token_rms(4, META)
            new_residual("mix_post_g", "ffn2_pre_g", META, 2 * KT, OUT_U + KT + 3)
            ffn(FFN2, META, 2 * KT, 5)
            token_rms(6, META)
            for g in range(len(RESULT) + 1):
                if g < len(RESULT):
                    k0, k1 = RESULT[g]
                    dve.wait_ge(out_gained, k1)
                    r = rms[:, META:T].rearrange("p (a t) -> p a t", a=1).to_broadcast([P, k1 - k0, SEQ])
                    dve.tensor_tensor(facc[:, k0:k1, META:T], facc[:, k0:k1, META:T], r, ALU.mult).then_inc(
                        out_scaled, 1)
                if g:
                    k0, k1 = RESULT[g - 1]
                    dve.wait_ge(out_scaled, g)
                    dve.tensor_tensor(facc[:, k0:k1, META:T], facc[:, k0:k1, META:T], h[:, k0:k1, META:T],
                                      ALU.add).then_inc(out_ready, 1)


def _tiles(v, n):
    return v.reshape(-1, n, P).transpose(2, 0, 1).reshape(P, -1)


def _by_output(w):
    n = w.shape[1] // P
    return w.reshape(-1, P, n, P).transpose(2, 1, 0, 3).reshape(n, P, -1)


def _ffn_units(np, gate, up, down):
    gu = np.stack([_by_output(gate), _by_output(up)], 1).reshape(2 * FT, P, UB * P)
    units, f0 = [], 0
    for nf in CHUNKS:
        units.append(gu[2 * f0:2 * (f0 + nf)])
        d = _by_output(down[f0 * P:(f0 + nf) * P]).reshape(KT, P, nf, P)
        units.append(d.transpose(0, 2, 1, 3).reshape(nf, UB, P, P).transpose(0, 2, 1, 3).reshape(nf, P, UB * P))
        f0 += nf
    return units


def kernel(**inputs):
    import numpy as np
    import concourse.bacc as bacc
    from concourse.bass_utils import run_bass_kernel_spmd

    a = {k: np.asarray(v) for k, v in inputs.items()}
    one = {k: v[0] for k, v in a.items() if k != "meta_tokens"}
    tokens = np.concatenate([a["meta_tokens"], one["x"]], 0)
    xt = tokens.T.reshape(KT, P, T).transpose(1, 0, 2)
    w_in = _by_output(one["w_in"]).reshape(5, LT, P, UB * P)[[1, 0, 2, 3, 4]].transpose(1, 0, 2, 3)
    weights = np.concatenate(
        _ffn_units(np, one["ffn1_w_gate"], one["ffn1_w_up"], one["ffn1_w_down"])
        + [w_in.reshape(5 * LT, P, UB * P), _by_output(one["w_out"])]
        + _ffn_units(np, one["ffn2_w_gate"], one["ffn2_w_up"], one["ffn2_w_down"]), 0)
    gates = np.stack([one["lru_w_a"], one["lru_w_x"]]).reshape(2, LT, P, HEAD).transpose(2, 0, 1, 3)
    vectors = np.concatenate([_tiles(one[k], one[k].shape[-1] // P) for k in VEC], 1)
    arrays = {"xt": xt, "weights": weights, "gates": gates, "vectors": vectors}
    arrays = {k: np.ascontiguousarray(v) for k, v in arrays.items()}

    nc = bacc.Bacc("TRN2", target_bir_lowering=False, num_devices=1)
    ins = [nc.dram_tensor(k, v.shape, mybir.dt.from_np(v.dtype), kind="ExternalInput").ap() for k, v in arrays.items()]
    out = nc.dram_tensor("out", (P, KT, SEQ), F32, kind="ExternalOutput").ap()
    hymba_layer_kernel(nc, *ins, out)
    got = run_bass_kernel_spmd(nc, [arrays], core_ids=[0]).results[0]["out"]
    return np.ascontiguousarray(got.transpose(2, 1, 0).reshape(1, SEQ, D))
```
